# Optimizing a Trainium2 kernel written in Bass

```python
import math
import jax, jax.numpy as jnp
from jax import lax
import numpy as np

D_MODEL = 1024
BATCH = 1
SEQ = 2048
DEPTH = 1

CHUNK = 64
Q_BLOCK = 128
ATT_HEADS = 4
ATT_HEAD_DIM = 64
ATT_V_DIM = 2 * ATT_HEAD_DIM
ATT_QK_WIDTH = 2 * ATT_HEADS * ATT_HEAD_DIM
ATT_WIDTH = ATT_HEADS * ATT_V_DIM
CONV_WIDTH = D_MODEL // 2
CONV_K = 3
ROPE_THETA = 500000.0
ROPE_DIM = ATT_HEAD_DIM // 4
NORM_EPS = 1e-6
SUBLN_EPS = 1e-5
N_BRANCH = 2
SPLIT_SIZES = (ATT_QK_WIDTH, ATT_QK_WIDTH, ATT_WIDTH, ATT_WIDTH,
               CONV_WIDTH, CONV_WIDTH, CONV_WIDTH, CONV_WIDTH,
               D_MODEL, D_MODEL)
IN_WIDTH = sum(SPLIT_SIZES)

kernel_name = "hybrid_diffattn_shortconv_gated_block"

def rmsnorm(x, w, eps):
    xf = x.astype(jnp.float32)
    xf = xf * lax.rsqrt(jnp.mean(xf * xf, axis=-1, keepdims=True) + eps)
    return (xf * w.astype(jnp.float32)).astype(x.dtype)

def partial_rotary(t, positions):
    half = ROPE_DIM // 2
    freqs = ROPE_THETA ** (-jnp.arange(0, ROPE_DIM, 2, dtype=jnp.float32) / ROPE_DIM)
    ang = positions.astype(jnp.float32)[..., None] * freqs
    cos = jnp.cos(ang)[:, :, None, :].astype(t.dtype)
    sin = jnp.sin(ang)[:, :, None, :].astype(t.dtype)
    t1, t2, rest = t[..., :half], t[..., half:ROPE_DIM], t[..., ROPE_DIM:]
    return jnp.concatenate([t1 * cos - t2 * sin, t2 * cos + t1 * sin, rest], axis=-1)

def diff_attention(q, k, v, positions, lam):
    b, s = q.shape[0], q.shape[1]
    nb = s // Q_BLOCK
    scale = 1.0 / math.sqrt(ATT_HEAD_DIM)
    k_chunk = positions // CHUNK
    q_blocks = jnp.moveaxis(q.reshape(b, nb, Q_BLOCK, 2 * ATT_HEADS, ATT_HEAD_DIM), 1, 0)
    p_blocks = jnp.moveaxis(positions.reshape(b, nb, Q_BLOCK), 1, 0)

    def one_block(args):
        qb, pb = args
        sc = jnp.einsum('bqhd,bkhd->bhqk', qb, k,
                        preferred_element_type=jnp.float32) * scale
        mask = k_chunk[:, None, None, :] <= (pb // CHUNK)[:, None, :, None]
        sc = jnp.where(mask, sc, jnp.finfo(jnp.float32).min)
        pr = jax.nn.softmax(sc, axis=-1).reshape(b, ATT_HEADS, 2, Q_BLOCK, s)
        a = pr[:, :, 0] - lam * pr[:, :, 1]
        return jnp.einsum('bhqk,bkhe->bqhe', a.astype(v.dtype), v)

    out = lax.map(one_block, (q_blocks, p_blocks))
    return jnp.moveaxis(out, 0, 1).reshape(b, s, ATT_HEADS, ATT_V_DIM)

def short_conv(u, w):
    return lax.conv_general_dilated(u, w.astype(u.dtype), window_strides=(1,),
                                    padding=[(CONV_K - 1, 0)],
                                    dimension_numbers=('NWC', 'WIO', 'NWC'),
                                    feature_group_count=CONV_WIDTH)

def setup_inputs(seed: int = 0) -> dict:
    key = jax.random.key(seed)
    ks = jax.random.split(key, 16)
    f32 = jnp.float32
    x = jax.random.normal(ks[0], (BATCH, SEQ, D_MODEL), f32)
    positions = jnp.broadcast_to(jnp.arange(SEQ, dtype=jnp.int32)[None, :], (BATCH, SEQ))
    pre_norm_w = 1.0 + 0.02 * jax.random.normal(ks[1], (DEPTH, D_MODEL), f32)
    w_in = jax.random.normal(ks[2], (DEPTH, D_MODEL, IN_WIDTH), f32) * D_MODEL ** -0.5
    merge_bias = 0.01 * jax.random.normal(ks[3], (DEPTH, N_BRANCH, D_MODEL), f32)
    lambda_q1 = 0.1 * jax.random.normal(ks[4], (DEPTH, ATT_HEAD_DIM), f32)
    lambda_k1 = 0.1 * jax.random.normal(ks[5], (DEPTH, ATT_HEAD_DIM), f32)
    lambda_q2 = 0.1 * jax.random.normal(ks[6], (DEPTH, ATT_HEAD_DIM), f32)
    lambda_k2 = 0.1 * jax.random.normal(ks[7], (DEPTH, ATT_HEAD_DIM), f32)
    subln_w = 1.0 + 0.02 * jax.random.normal(ks[8], (DEPTH, ATT_V_DIM), f32)
    w_att_out = jax.random.normal(ks[9], (DEPTH, ATT_WIDTH, D_MODEL), f32) * ATT_WIDTH ** -0.5
    conv_w = jax.random.normal(ks[10], (DEPTH, CONV_K, 1, CONV_WIDTH), f32) * CONV_K ** -0.5
    w_conv_out = jax.random.normal(ks[11], (DEPTH, CONV_WIDTH, D_MODEL), f32) * CONV_WIDTH ** -0.5
    w_out = jax.random.normal(ks[12], (DEPTH, D_MODEL, D_MODEL), f32) * D_MODEL ** -0.5
    post_norm_w = 1.0 + 0.02 * jax.random.normal(ks[13], (DEPTH, D_MODEL), f32)
    return {"x": x, "positions": positions, "pre_norm_w": pre_norm_w, "w_in": w_in,
            "merge_bias": merge_bias, "lambda_q1": lambda_q1, "lambda_k1": lambda_k1,
            "lambda_q2": lambda_q2, "lambda_k2": lambda_k2, "subln_w": subln_w,
            "w_att_out": w_att_out, "conv_w": conv_w, "w_conv_out": w_conv_out,
            "w_out": w_out, "post_norm_w": post_norm_w}

def reference(x, positions, pre_norm_w, w_in, merge_bias, lambda_q1, lambda_k1,
              lambda_q2, lambda_k2, subln_w, w_att_out, conv_w, w_conv_out,
              w_out, post_norm_w):
    b, s, _ = x.shape
    split_idx = list(np.cumsum(SPLIT_SIZES)[:-1])
    for layer in range(DEPTH):
        lambda_init = 0.8 - 0.6 * math.exp(-0.3 * layer)
        h = rmsnorm(x, pre_norm_w[layer], NORM_EPS)
        proj = h @ w_in[layer]
        (q, k, v, z_att, gb, gc, u, z_conv, g_att, g_conv) = jnp.split(proj, split_idx, axis=-1)

        q = partial_rotary(q.reshape(b, s, 2 * ATT_HEADS, ATT_HEAD_DIM), positions)
        k = partial_rotary(k.reshape(b, s, 2 * ATT_HEADS, ATT_HEAD_DIM), positions)
        v = v.reshape(b, s, ATT_HEADS, ATT_V_DIM)
        lam = (jnp.exp(jnp.sum(lambda_q1[layer].astype(jnp.float32) * lambda_k1[layer].astype(jnp.float32)))
               - jnp.exp(jnp.sum(lambda_q2[layer].astype(jnp.float32) * lambda_k2[layer].astype(jnp.float32)))
               + lambda_init)
        att = diff_attention(q, k, v, positions, lam)
        att = rmsnorm(att, subln_w[layer], SUBLN_EPS) * (1.0 - lambda_init)
        att = att.reshape(b, s, ATT_WIDTH) * jax.nn.silu(z_att)
        y_att = att @ w_att_out[layer]

        cv = gb * short_conv(gc * u, conv_w[layer])
        y_conv = (cv * jax.nn.silu(z_conv)) @ w_conv_out[layer]

        m = (jax.nn.sigmoid(g_att + merge_bias[layer, 0]) * y_att
             + jax.nn.sigmoid(g_conv + merge_bias[layer, 1]) * y_conv)
        x = x + rmsnorm(m @ w_out[layer], post_norm_w[layer], NORM_EPS)
    return x


_drawn_inputs = setup_inputs


def setup_inputs(seed=0):
    import zlib

    import numpy as np

    out = dict(_drawn_inputs(seed))
    spreads = {}
    factors = {'merge_bias': 8.0,
     'lambda_k1': 3.875,
     'lambda_q2': 4.14,
     'subln_w': 5.938,
     'post_norm_w': 3.885}
    for name, (base, spread) in spreads.items():
        noise = np.random.default_rng([zlib.crc32(name.encode()), seed]).standard_normal(out[name].shape)
        drawn = base * np.exp(spread * noise) if base else spread * noise
        out[name] = __import__('jax').numpy.asarray(drawn.astype(out[name].dtype))
    for name, factor in factors.items():
        out[name] = (out[name] * factor).astype(out[name].dtype)
    return out
```

```python
from contextlib import ExitStack

import numpy as np

import concourse.bass as bass
import concourse.mybir as mybir
from concourse.alu_op_type import AluOpType as ALU

ACT = mybir.ActivationFunctionType
F32 = mybir.dt.float32
F32R = mybir.dt.float32r
I32 = mybir.dt.int32
AX_X = mybir.AxisListType.X

P = 128
D = 1024
S = 2048
KT = D // P
CHUNK = 64
CHUNK_SHIFT = 6
VH = 4
SH = 2 * VH
HD = 64
VD = 128
WIDTH = 512
ROPE = HD // 4
HALF = ROPE // 2
REST = HD - ROPE
THETA = 500000.0
EPS = 1e-6
SUB_EPS = 1e-5
LAMBDA_INIT = 0.8 - 0.6
SCALE = HD ** -0.5
MASKED = -1e30
LOWEST = -3e38

BLK = 512
NB = S // BLK
NT = S // P
QPB = BLK // P

QK_TILES = 8
Z_TILES = 4
CONV_TILES = 16
GATE_TILES = 16
N_TILES = QK_TILES + Z_TILES + CONV_TILES + GATE_TILES
Z0 = QK_TILES
C0 = Z0 + Z_TILES
G0 = C0 + CONV_TILES

TURN = (6.28125, 0.00193500518798828125, 3.01991693e-07)
ROUND = 1.5 * 2 ** 23
PI_BELOW = 3.1415925

PAIR_BLOCKS = NT // 2
QB = 2 * P


def build(nc, t):
    with ExitStack() as whole:
        def sem(name):
            return whole.enter_context(nc.semaphore(name))

        def held(name, shape, dt=F32, ctx=whole):
            return ctx.enter_context(nc.sbuf_tensor(name, shape, dt))

        def scratch(name, shape):
            return nc.dram_tensor(name, shape, F32, kind="Internal").ap()

        bank = [whole.enter_context(nc.psum_tensor(f"bank{i}", [P, 512], F32)) for i in range(8)]

        qk_s = scratch("qk_s", [2, 2 * WIDTH, S])
        v_s = scratch("v_s", [2, S, WIDTH])
        z_s = scratch("z_s", [WIDTH, S])
        cv_s = scratch("cv_s", [2, WIDTH, S])
        gate_s = scratch("gate_s", [2 * D, S])
        att_s = scratch("att_s", [2, WIDTH, S])

        ident = held("ident", [P, P])
        ones = held("ones", [P, P])
        zeros = held("zeros", [P, 512])
        lam = held("lam", [P, 8])
        eps = held("eps", [P, 1])
        causal_flag = held("causal_flag", [P, 1], I32)
        sub_w = held("sub_w", [P, 2])

        early = ExitStack()
        sub = ExitStack()
        wv_hi = held("wv_hi", [P, KT, WIDTH], F32R, sub)
        wv_lo = held("wv_lo", [P, KT, WIDTH], F32R, sub)
        sub.close()
        cos_t = held("cos_t", [P, S], F32, early)
        sin_t = held("sin_t", [P, S], F32, early)
        cu = held("cu", [P, S + 2], F32, early)
        tmp = [held(f"tmp{i}", [P, BLK], F32, early) for i in range(3)]
        held("rest_of_wv", [P, 2 * KT * WIDTH - 3 * S - 2 - 3 * BLK], F32, early)
        ht_hi = held("ht_hi", [P, KT, S], F32R, early)
        ht_lo = held("ht_lo", [P, KT, S], F32R, early)
        raw = [held(f"raw{i}", [P, D], F32, early) for i in range(2)]
        stage = [held(f"stage{i}", [P, 2, BLK], F32, early) for i in range(4)]
        rope_cols = held("rope_cols", [P, 2], F32, early)
        bias = held("bias", [P, GATE_TILES], F32, early)
        conv_w = held("conv_w", [P, 4, 3], F32, early)
        sums = held("sums", [P, 3, NT], F32, early)
        norm_w = held("norm_w", [P, D], F32, early)
        sub = ExitStack()
        x_in = [held(f"x_in{i}", [P, D], F32, sub) for i in range(2)]
        x_n = [held(f"x_n{i}", [P, D], F32, sub) for i in range(2)]
        sub.close()
        w_hi = [held(f"w_hi{i}", [P, KT, P], F32R, early) for i in range(2)]
        w_lo = [held(f"w_lo{i}", [P, KT, P], F32R, early) for i in range(2)]
        early.close()

        mid = ExitStack()
        kc = held("kc", [P, S], F32, mid)
        q_st = [held(f"q_st{b}", [P, 2, BLK], F32R, mid) for b in range(2)]
        k_sl = [held("k_sl0", [P, 2, 2, BLK], F32R, mid)]
        v_sl = [held("v_sl0", [P, 2, QPB, VD], F32R, mid)]
        lvec = held("lvec", [P, 4, HD], F32, mid)
        qc = held("qc", [P, NT], F32, mid)
        flags = held("flags", [P, 4, NT], F32, mid)
        eps_fill = held("eps_fill", [P, P], F32, mid)
        k_sl += [held(f"k_sl{i}", [P, 2, 2, BLK], F32R, mid) for i in range(1, 5)]
        v_sl += [held(f"v_sl{i}", [P, 2, QPB, VD], F32R, mid) for i in range(1, 5)]
        e1 = [held(f"e1_{b}", [P, S], F32, mid) for b in range(3)]
        e2 = [held(f"e2_{b}", [P, S], F32, mid) for b in range(2)]
        at_hi = [held(f"at_hi{b}", [P, NT, QB], F32R, mid) for b in range(2)]
        at_lo = [held(f"at_lo{b}", [P, NT, QB], F32R, mid) for b in range(2)]
        mask = [held(f"mask{b}", [P, BLK], F32, mid) for b in range(2)]
        mx = held("mx", [P, 2, NB], F32, mid)
        m2 = held("m2", [P, 2], F32, mid)
        nbias = [held(f"nbias{b}", [P, 2], F32, mid) for b in range(2)]
        esum = [held(f"esum{b}", [P, 2], F32, mid) for b in range(2)]
        ratio = held("ratio", [P, 2], F32, mid)
        es = [held(f"es{i}", [P, P], F32, mid) for i in range(4)]
        z_in = [held(f"z_in{b}", [P, QB], F32, mid) for b in range(2)]
        o_sq = held("o_sq", [P, QB], F32, mid)
        o_r = held("o_r", [P, QB], F32, mid)
        o_n = held("o_n", [P, QB], F32, mid)
        o_st = [held(f"o_st{b}", [P, 2, QB], F32, mid) for b in range(2)]
        mid.close()

        late = ExitStack()
        wa_hi = held("wa_hi", [P, 8, D], F32R, late)
        wo_hi = held("wo_hi", [P, KT, D], F32R, late)
        sub = ExitStack()
        wa_raw = held("wa_raw", [P, 8, D], F32, sub)
        wo_raw = held("wo_raw", [P, KT, D], F32, sub)
        sub.close()
        wa_lo = held("wa_lo", [P, 8, D], F32R, late)
        wo_lo = held("wo_lo", [P, KT, D], F32R, late)
        br_hi = held("br_hi", [P, 8, BLK], F32R, late)
        br_lo = held("br_lo", [P, 8, BLK], F32R, late)
        m_hi = held("m_hi", [P, KT, BLK], F32R, late)
        m_lo = held("m_lo", [P, KT, BLK], F32R, late)
        ring = [held(f"ring{i}", [P, BLK], F32, late) for i in range(4)]
        post_w = held("post_w", [P, D], F32, late)
        y_ss = [held(f"y_ss{i}", [P, 4], F32, late) for i in range(2)]
        late.close()

        norm_in, small_in, cols_in = sem("norm_in"), sem("small_in"), sem("cols_in")
        pos_in = sem("pos_in")
        consts_ready = sem("consts_ready")
        lam_step = sem("lam_step")
        x_loaded = [sem(f"x_loaded{i}") for i in range(2)]
        x_squared, x_rooted, x_recip, x_normed = (
            sem("x_squared"), sem("x_rooted"), sem("x_recip"), sem("x_normed"))
        x_turned, ht_hi_done, ht_lo_done = sem("x_turned"), sem("ht_hi_done"), sem("ht_lo_done")
        raw_loaded = [sem(f"raw_loaded{i}") for i in range(2)]
        w_hi_done, w_lo_done = sem("w_hi_done"), sem("w_lo_done")
        v_done, v_hi_out = sem("v_done"), sem("v_hi_out")
        table_step, table_sin = sem("table_step"), sem("table_sin")
        proj_done = sem("proj_done")
        dve_done, gate_done = sem("dve_done"), sem("gate_done")
        hi_done, sig_done = sem("hi_done"), sem("sig_done")
        rot_cos, rot_sin, rot_sum = sem("rot_cos"), sem("rot_sin"), sem("rot_sum")
        tap0, tap1, tap2, silu_done, cv_done = (
            sem("tap0"), sem("tap1"), sem("tap2"), sem("silu_done"), sem("cv_done"))
        stored = [sem(f"stored{i}") for i in range(4)]

        k_loaded = [sem(f"k_loaded{i}") for i in range(5)]
        v_loaded = [sem(f"v_loaded{i}") for i in range(5)]
        q_loaded = [sem(f"q_loaded{i}") for i in range(2)]
        z_loaded = [sem(f"z_loaded{i}") for i in range(2)]
        chunk_in, chunk_step = sem("chunk_in"), sem("chunk_step")
        flag_step, flag_ready = sem("flag_step"), sem("flag_ready")
        qk_done, scored, reduced, nb_ready = sem("qk_done"), sem("scored"), sem("reduced"), sem("nb_ready")
        mask_ready, exp_done, recip_done, ratio_ready = (
            sem("mask_ready"), sem("exp_done"), sem("recip_done"), sem("ratio_ready"))
        combined, es_ready = sem("combined"), sem("es_ready")
        turned, at_hi_done, at_lo_done = sem("turned"), sem("at_hi_done"), sem("at_lo_done")
        pv_done, sq_done, ss_done, ln_done, r_done = (
            sem("pv_done"), sem("sq_done"), sem("ss_done"), sem("ln_done"), sem("r_done"))
        o_normed, o_gated, o_hi_done, o_lo_done = (
            sem("o_normed"), sem("o_gated"), sem("o_hi_done"), sem("o_lo_done"))
        att_stored = [sem(f"att_stored{i}") for i in range(2)]

        w3_loaded = [sem(f"w3_loaded{i}") for i in range(16)]
        post_in = sem("post_in")
        w3_hi_done, w3_lo_done = sem("w3_hi_done"), sem("w3_lo_done")
        br_loaded = sem("br_loaded")
        ring_loaded = [sem(f"ring_loaded{i}") for i in range(4)]
        y_done, y_gated, m_sum, m_hi_done, m_lo_done = (
            sem("y_done"), sem("y_gated"), sem("m_sum"), sem("m_hi_done"), sem("m_lo_done"))
        f_done, f_sq, f_sum, f_root, f_recip, f_scaled, f_out = (
            sem("f_done"), sem("f_sq"), sem("f_sum"), sem("f_root"), sem("f_recip"),
            sem("f_scaled"), sem("f_out"))
        y_stored = [sem(f"y_stored{i}") for i in range(4)]

        ahead = [proj_done, scored, combined, ss_done, es_ready, o_gated, o_lo_done, at_lo_done, o_normed,
                 ln_done, pv_done, turned, y_gated, y_done, f_done, f_out, f_sq]
        ahead_dma = att_stored + y_stored

        block = whole.enter_context(nc.Block())

        SECTIONS = [(0, 2, 4, "qk"), (Z0, 2, 2, "z"), (C0, 4, 4, "conv"),
                    (G0, 1, 2, "gate"), (G0 + 2, 6, 2, "gate"), (G0 + 14, 1, 2, "gate")]

        def sections(eng, body):
            for first, iters, width, kind in SECTIONS:
                if iters == 1:
                    for j in range(width):
                        body(first + j, j, 0, kind, first)
                else:
                    with eng.Fori(0, iters) as it:
                        for j in range(width):
                            body(it * width + (first + j), j, it, kind, first)

        def by_plan(eng, attend):
            eng.wait_ge(flag_ready, 1)
            causal = eng.value_load(causal_flag[0:1, 0:1], min_val=0, max_val=1)
            with eng.If(causal == 1):
                attend(Plan(True))
            with eng.Else():
                attend(Plan(False))

        def is_last(first, j, ahead):
            return first == G0 + 14 and j + ahead >= 2

        TO_Z = NT // 4 + QK_TILES + 2 * 3
        TO_GATES = TO_Z + Z_TILES + 4

        def stores_before(n, j, it, kind):
            if kind == "qk":
                return n + it * 3 + (NT // 4 + (3 if j else 0))
            if kind == "z":
                return n + (TO_Z - Z0)
            if kind == "conv":
                return it + (TO_Z + Z_TILES)
            return n + (TO_GATES - G0)

        def done_before(n):
            return n * NB + NT

        PER = 2 * NT
        K_IN, V_IN, Q_IN = 8 * 16, 2 * 16, 4 * 16

        class Plan:
            def __init__(self, causal):
                self.causal = causal
                self.CH = self.before(PER)
                self.MASKS = self.masks_before(PER)

            def keys(self, L):
                return P * (L % NT + 1) if self.causal else S

            def chunks(self, L):
                n = self.keys(L)
                return [(c, min(BLK, n - c)) for c in range(0, n, BLK)]

            def masked(self, L, c):
                return not self.causal or c == self.chunks(L)[-1][0]

            def before(self, L):
                return sum(len(self.chunks(x)) for x in range(L))

            def masks_before(self, L):
                return sum(self.masked(x, c) for x in range(L) for c, _ in self.chunks(x))

            def first_use(self, L, c):
                return L % NT == (c // P if self.causal else 0)

            def round(self, L):
                s_items = [("s", c, w, h) for c, w in self.chunks(L + 1) for h in range(2)] if L + 1 < PER else []
                t_items = [("t", c, w) for c, w in self.chunks(L - 1)] if 1 <= L <= PER else []
                out = []
                while s_items or t_items:
                    out += s_items[:2] + t_items[:1]
                    s_items, t_items = s_items[2:], t_items[1:]
                return out or [("",)]

        def slot(L, c):
            return (L // NT, 1) if c == 0 else (1 + c // BLK, 2)

        def loads(it, L, c):
            return it + 1 if c == 0 else 2 * it + (L // NT + 1)

        @block.sync
        def _(sp):
            sp.dma_start(norm_w[:], t["pre_norm_w"].to_broadcast([P, D])).then_inc(norm_in, 16)
            def load_x(i):
                if i >= 2:
                    sp.wait_ge(x_normed, i - 1)
                sp.dma_start(x_in[i % 2][:], t["x"][i * P:(i + 1) * P, :]).then_inc(x_loaded[i % 2], 16)

            load_x(0)
            load_x(1)
            sp.dma_start(raw[0][:], t["w_v"][0]).then_inc(raw_loaded[0], 16)
            sp.dma_start(raw[1][:], t["w_v"][1]).then_inc(raw_loaded[1], 16)
            sp.dma_start(rope_cols[:], t["rope_cols"]).then_inc(cols_in, 16)
            sp.dma_start(bias[:], t["bias"]).then_inc(cols_in, 16)
            sp.dma_start(conv_w[:], t["conv_w"]).then_inc(cols_in, 16)
            load_x(2)
            for i in range(2, 4):
                sp.wait_ge(w_lo_done, i - 1)
                sp.wait_ge(w_hi_done, i - 1)
                sp.dma_start(raw[i % 2][:], t["w_v"][i]).then_inc(raw_loaded[i % 2], 16)
                load_x(i + 1)
            for i in range(2):
                sp.wait_ge(w_lo_done, i + 3)
                sp.wait_ge(w_hi_done, i + 3)
                sp.dma_start(raw[i][:], t["w_in"][i * P:(i + 1) * P, :]).then_inc(raw_loaded[i], 16)
                load_x(5 + i)

            def store_v(i):
                sp.wait_ge(dve_done, i + 1)
                sp.dma_start(v_s[:, i * P:(i + 1) * P, :].rearrange("s p e -> p s e"),
                             stage[i % 4][:]).then_inc(stored[i % 4], 16)

            for i in range(NT):
                if i + 7 < NT:
                    load_x(i + 7)
                store_v(i)
                if i == NT - 1:
                    sp.wait_ge(v_done, NT)
                    sp.dma_start(cos_t[:].bitcast(I32), t["positions"].to_broadcast([P, S])).then_inc(pos_in, 16)

            def rows_in(dst, which, half, pair, cs, done):
                head = 2 * pair
                src = qk_s[half, which * WIDTH:(which + 1) * WIDTH, cs]
                sp.dma_start(dst[0:ROPE], src[head * ROPE:(head + 2) * ROPE, :].rearrange("(h j) n -> j h n", h=2)
                             ).then_inc(done, 16)
                sp.dma_start(dst[ROPE:HD], src[P + head * REST:P + (head + 2) * REST, :]
                             .rearrange("(h j) n -> j h n", h=2)).then_inc(done, 16)

            def load_k(pair, c):
                sl = slot(NT * (pair % 2), c)[0]
                for at in (0, HD):
                    for half in range(2):
                        rows_in(k_sl[sl][at:at + HD, half].bitcast(F32), 1, half, pair, slice(c, c + BLK),
                                k_loaded[sl])

            def load_v(pair, c):
                sl = slot(NT * (pair % 2), c)[0]
                for half in range(2):
                    sp.dma_start(v_sl[sl][:, half].bitcast(F32),
                                 v_s[half, c:c + BLK, pair * VD:(pair + 1) * VD].rearrange("(t p) e -> p t e", p=P)
                                 ).then_inc(v_loaded[sl], 16)

            def load_q(group):
                pair, g = divmod(group, NB)
                for half in range(2):
                    rows_in(q_st[g % 2][half * HD:(half + 1) * HD].bitcast(F32), 0, half, pair,
                            slice(g * BLK, (g + 1) * BLK), q_loaded[g % 2])

            def attend_first():
                sp.wait_ge(dve_done, done_before(G0))
                for s_ in stored:
                    sp.wait_ge(s_, 16 * TO_GATES)
                sp.dma_start(kc[:].bitcast(I32), t["positions"].to_broadcast([P, S])).then_inc(chunk_in, 16)
                sp.dma_start(qc[:].bitcast(I32), t["positions_by_tile"]).then_inc(chunk_in, 16)
                for i, name in enumerate(("lambda_q1", "lambda_k1", "lambda_q2", "lambda_k2")):
                    sp.dma_start(lvec[:, i, :], t[name].to_broadcast([P, HD])).then_inc(small_in, 16)
                sp.dma_start(sub_w[:, 0:1], t["subln_w"]).then_inc(small_in, 16)
                load_q(0)
                load_k(0, 0)
                load_q(1)
                load_v(0, 0)

            def project(n, j, it, kind, first):
                if not is_last(first, j, 2):
                    sp.wait_ge(w_hi_done, n + 5)
                    sp.wait_ge(w_lo_done, n + 5)
                    sp.dma_start(raw[j % 2][:], t["w_in"][bass.ds((n + 2) * P, P), :]
                                 ).then_inc(raw_loaded[j % 2], 16)
                if kind == "conv" and j != 3:
                    return
                if first == G0 and j == 0:
                    attend_first()
                for b in range(NB):
                    cs = slice(b * BLK, (b + 1) * BLK)
                    if kind != "gate":
                        sp.wait_ge(dve_done, done_before(n) + (b + 1))
                    if kind == "gate":
                        sp.wait_ge(gate_done, (n - G0) * NB + (b + 1))
                        sp.dma_start(gate_s[bass.ds((n - G0) * P, P), cs], stage[b][:, 0, :]
                                     ).then_inc(stored[b], 16)
                    elif kind == "z":
                        sp.dma_start(z_s[bass.ds((n - Z0) * P, P), cs], stage[b][:, 0, :]
                                     ).then_inc(stored[b], 16)
                    elif kind == "conv":
                        sp.dma_start(cv_s[:, bass.ds(it * P, P), cs].rearrange("s p e -> p s e"),
                                     stage[b][:]).then_inc(stored[b], 16)
                    elif j:
                        sp.dma_start(qk_s[:, bass.ds(it * WIDTH + j * P, P), cs].rearrange("s p e -> p s e"),
                                     stage[b][:]).then_inc(stored[b], 16)
                    else:
                        for half in range(2):
                            rows = qk_s[half, bass.ds(it * WIDTH, P), cs].rearrange("(h a i) n -> a h i n", a=2, i=HALF)
                            for a in range(2):
                                sp.dma_start(rows[a], stage[b][a * HD:(a + 1) * HD, half, :]).then_inc(stored[b], 16)

            sections(sp, project)

            for s_ in stored:
                sp.wait_ge(s_, 16 * (TO_GATES + GATE_TILES))
            for c in range(BLK, S, BLK):
                load_k(0, c)
                load_v(0, c)
            load_k(1, 0)
            load_v(1, 0)

            def store_att(B):
                pr, bb = divmod(B, PAIR_BLOCKS)
                sp.wait_ge(o_lo_done, 1 + B + 1)
                sp.dma_start(att_s[:, pr * VD:(pr + 1) * VD, bb * QB:(bb + 1) * QB].rearrange("s p e -> p s e"),
                             o_st[B % 2][:]).then_inc(att_stored[B % 2], 16)

            def attend(plan):
                for G in range(VH * NT):
                    pair, ti = divmod(G, NT)
                    it, L = divmod(G, PER)
                    if ti % QPB == 0 and QPB <= G < VH * NT - QPB:
                        sp.wait_ge(qk_done, 2 * (it * plan.CH + plan.before(L)))
                        load_q(G // QPB + 1)
                    if ti == 1 and pair in (1, 2):
                        sp.wait_ge(pv_done, 1 + PAIR_BLOCKS * pair)
                        load_k(pair + 1, 0)
                        load_v(pair + 1, 0)
                    if ti == 2 and pair:
                        sp.wait_ge(pv_done, 1 + PAIR_BLOCKS * pair)
                        for c in range(BLK, S, BLK):
                            load_v(pair, c)
                    if ti == NT - 1 and pair < VH - 1:
                        sp.wait_ge(qk_done, 2 * (it * plan.CH + plan.before(L + 1)))
                        for c in range(BLK, S, BLK):
                            load_k(pair + 1, c)
                    if G % 2 == 0:
                        B = G // 2
                        if B >= 2:
                            sp.wait_ge(o_gated, 1 + B - 1)
                        b0 = (B % PAIR_BLOCKS) * QB
                        sp.dma_start(z_in[B % 2][:], z_s[pair * VD:(pair + 1) * VD, b0:b0 + QB]
                                     ).then_inc(z_loaded[B % 2], 16)
                    elif G >= 7:
                        store_att((G - 7) // 2)
                for B in range(VH * PAIR_BLOCKS - 3, VH * PAIR_BLOCKS):
                    store_att(B)

            by_plan(sp, attend)

            for s_ in att_stored:
                sp.wait_ge(s_, 16 + 16 * VH * PAIR_BLOCKS // 2)
            def load_branches(b):
                for half, dst in ((0, br_hi), (1, br_lo)):
                    for k0, src in ((0, att_s), (4, cv_s)):
                        sp.dma_start(dst[:, k0:k0 + 4, :].bitcast(F32),
                                     src[half, :, bass.ds(b * BLK, BLK)].rearrange("(k p) n -> p k n", p=P)
                                     ).then_inc(br_loaded, 16)

            for i in range(8):
                k0, cs = 2 * (i % 4), slice(i // 4 * 512, i // 4 * 512 + 512)
                src = (t["w_att_out"] if k0 < 4 else t["w_conv_out"])[k0 % 4 * P:(k0 % 4 + 2) * P, cs]
                sp.dma_start(wa_raw[:, k0:k0 + 2, cs], src.rearrange("(k p) n -> p k n", p=P)
                             ).then_inc(w3_loaded[i], 16)
                if i == 3:
                    load_branches(0)

            sp.dma_start(post_w[:], t["post_norm_w"].to_broadcast([P, D])).then_inc(post_in, 16)

            def ring_load(b, i):
                if i < 16:
                    src = gate_s[(i % 2) * D + (i // 2) * P:(i % 2) * D + (i // 2 + 1) * P, bass.ds(b * BLK, BLK)]
                else:
                    src = t["x"][bass.ds(b * BLK + ((i - 16) // 2) * P, P), (i % 2) * 512:(i % 2) * 512 + 512]
                sp.dma_start(ring[i % 4][:], src).then_inc(ring_loaded[i % 4], 16)

            def store_rows(b, i):
                sp.wait_ge(f_out, 1 + b * 8 + (i + 1))
                sp.dma_start(t["out"][bass.ds(b * BLK + (i // 2) * P, P), (i % 2) * 512:(i % 2) * 512 + 512],
                             ring[i % 4][:]).then_inc(y_stored[i % 4], 16)

            def merge(b, first=False, last=False):
                for i in range(20):
                    if i < 4:
                        sp.wait_ge(y_stored[i], 16 + b * 32)
                    else:
                        sp.wait_ge(m_lo_done, b * KT + (i - 4) // 2 + 1)
                    ring_load(b, i)
                    if first and i == 3:
                        for k in range(KT):
                            sp.dma_start(wo_raw[:, k, :], t["w_out"][k * P:(k + 1) * P, :]
                                         ).then_inc(w3_loaded[8 + k], 16)
                if not last:
                    sp.wait_ge(y_done, 1 + (b + 1) * 2 * KT)
                    load_branches(b + 1)
                for i in range(4):
                    store_rows(b, i)
                    sp.wait_ge(y_stored[i], 16 + b * 32 + 16)
                    ring_load(b, 20 + i)
                for i in range(4, 8):
                    store_rows(b, i)

            merge(0, first=True)
            with sp.Fori(1, NB - 1) as b:
                merge(b)
            merge(NB - 1, last=True)
            for s_ in y_stored:
                sp.wait_ge(s_, 16 + 32 * NB)

        @block.gpsimd
        def _(pool):
            for s_ in ahead:
                pool.sem_inc(s_, 1)
            for s_ in ahead_dma:
                pool.sem_inc(s_, 16)
            nc.gpsimd.memset(ident[:], 0.0).then_inc(consts_ready, 1)
            nc.gpsimd.memset(ones[:], 1.0).then_inc(consts_ready, 1)
            nc.gpsimd.memset(zeros[:], 0.0).then_inc(consts_ready, 1)
            nc.gpsimd.memset(eps[:], EPS).then_inc(consts_ready, 1)
            pool.wait_ge(consts_ready, 4)
            nc.gpsimd.affine_select(out=ident[:], in_=ident[:], compare_op=ALU.not_equal, fill=1.0, base=0,
                                    pattern=[[-1, P]], channel_multiplier=1).then_inc(consts_ready, 1)

            pool.wait_ge(chunk_step, 4)
            for s_ in stored:
                pool.wait_ge(s_, 16 * (TO_GATES + GATE_TILES))

            def attend(plan):
                with pool.Fori(0, 2) as it:
                    freed = [0, 0]
                    m = 0
                    for L in range(PER):
                        for i, (c, w) in enumerate(plan.chunks(L)):
                            if not plan.masked(L, c):
                                continue
                            pool.wait_ge(scored, 1 + it * 2 * plan.CH + freed[m % 2])
                            nc.gpsimd.nop(nofuse=True)
                            nc.gpsimd.tensor_scalar(mask[m % 2][:, 0:w], kc[:, c:c + w], qc[:, L % NT:L % NT + 1],
                                                    MASKED, ALU.is_gt, ALU.mult).then_inc(mask_ready, 1)
                            freed[m % 2] = 2 * (plan.before(L) + i + 1)
                            m += 1

            by_plan(pool, attend)

        @block.tensor
        def _(pe):
            def split_product(out, w, x, start=True, stop=True):
                nc.tensor.matmul(out, w[0], x[0], start=start, stop=False)
                nc.tensor.matmul(out, w[0], x[1], start=False, stop=False)
                return nc.tensor.matmul(out, w[1], x[0], start=False, stop=stop)

            def turn_x(i):
                pe.wait_ge(x_normed, i + 1)
                if i >= 2:
                    pe.wait_ge(ht_lo_done, 2 * (i - 1))
                for g in range(2):
                    for k in range(4):
                        mm = nc.tensor.transpose(bank[2 * (i % 2) + g][:, k * P:(k + 1) * P],
                                                 x_n[i % 2][:, (4 * g + k) * P:(4 * g + k + 1) * P], ident[:])
                    mm.then_inc(x_turned, 1)

            pe.wait_ge(consts_ready, 5)
            turn_x(0)
            turn_x(1)
            for i in range(NT):
                if i + 2 < NT:
                    turn_x(i + 2)
                if i == 0:
                    pe.wait_ge(w_lo_done, 4)
                    pe.wait_ge(w_hi_done, 4)
                pe.wait_ge(ht_lo_done, 2 * (i + 1))
                if i >= 4:
                    pe.wait_ge(dve_done, i - 3)
                cs = slice(i * P, (i + 1) * P)
                for k in range(KT):
                    mm = split_product(bank[4 + i % 4][:], (ht_hi[:, k, cs], ht_lo[:, k, cs]),
                                       (wv_hi[:, k, :], wv_lo[:, k, :]), k == 0, k == KT - 1)
                mm.then_inc(v_done, 1)

            def project(n, j, it, kind, first):
                pe.wait_ge(w_hi_done, n + 5)
                pe.wait_ge(w_lo_done, n + 5)
                for b in range(NB):
                    if first >= G0 + 2:
                        pe.wait_ge(gate_done, (n - G0 - 2) * NB + (b + 1))
                    else:
                        pe.wait_ge(dve_done, n * NB + (NT - 2 * NB + b + 1))
                    cs = slice(b * BLK, (b + 1) * BLK)
                    for k in range(KT):
                        mm = split_product(bank[4 * (j % 2) + b][:], (w_hi[j % 2][:, k, :], w_lo[j % 2][:, k, :]),
                                           (ht_hi[:, k, cs], ht_lo[:, k, cs]), k == 0, k == KT - 1)
                    mm.then_inc(proj_done, 1)

            sections(pe, project)

            for s_ in stored:
                pe.wait_ge(s_, 16 * (TO_GATES + GATE_TILES))

            def attend(plan):
                def score(it, L, c, w, h):
                    ti = L % NT
                    sl, per = slot(L, c)
                    if h == 0 and plan.first_use(L, c):
                        pe.wait_ge(k_loaded[sl], loads(it, L, c) * K_IN)
                    if ti % QPB == 0 and c == 0 and h == 0:
                        pe.wait_ge(q_loaded[L // QPB % 2], (it * 4 + (L // QPB // 2 + 1)) * Q_IN)
                    o = 2 * (plan.before(L) + c // BLK) + h
                    pe.wait_ge(scored, 1 + it * 2 * plan.CH + max(o - 3, 0))
                    q = q_st[L // QPB % 2][:, h, (ti % QPB) * P:(ti % QPB + 1) * P]
                    nc.tensor.matmul(bank[o % 4][:, 0:w], q, k_sl[sl][:, 0, h, 0:w], start=True, stop=False)
                    nc.tensor.matmul(bank[o % 4][:, 0:w], q, k_sl[sl][:, 1, h, 0:w], start=False,
                                     stop=True).then_inc(qk_done, 1)

                def turn(it, L, c, w):
                    if c == 0:
                        pe.wait_ge(combined, 1 + it * PER + (L + 1))
                    o = plan.before(L) + c // BLK
                    pe.wait_ge(at_lo_done, 1 + it * plan.CH + max(o - 1, 0))
                    for k in range(w // P):
                        mm = nc.tensor.transpose(bank[4 + o % 2][:, k * P:(k + 1) * P],
                                                 e1[L % 3][:, c + k * P:c + (k + 1) * P], ident[:])
                    mm.then_inc(turned, 1)

                def values(it, L, share, shares):
                    B = L // 2
                    n = plan.keys(L) // P
                    order = [(0, 0)] + [(k, x) for k in range(n - 1, 0, -1) for x in range(3)] + [(0, 1), (0, 2)]
                    if share == 0:
                        values_ready(it, L)
                    for i in range(len(order) * share // shares, len(order) * (share + 1) // shares):
                        k, x = order[i]
                        q0 = P if plan.causal and k == n - 1 else 0
                        v = v_sl[slot(L, k // QPB * BLK)[0]][:, x // 2, k % QPB, :]
                        a = (at_lo if x == 1 else at_hi)[B % 2]
                        mm = nc.tensor.matmul(bank[6][:, q0:QB], v, a[:, k, q0:QB], start=i == 0,
                                              stop=i == len(order) - 1)
                    if share == shares - 1:
                        mm.then_inc(pv_done, 1)

                def values_ready(it, L):
                    B = L // 2
                    pe.wait_ge(at_lo_done, 1 + it * plan.CH + plan.before(L + 1))
                    pe.wait_ge(o_normed, 1 + it * (PER // 2) + B)
                    for c, w in plan.chunks(L):
                        if plan.first_use(L, c) or plan.first_use(L - 1, c):
                            pe.wait_ge(v_loaded[slot(L, c)[0]], loads(it, L, c) * V_IN)

                def square_sums(it, B):
                    pe.wait_ge(sq_done, it * (PER // 2) + (B + 1))
                    pe.wait_ge(ln_done, 1 + it * (PER // 2) + B)
                    pe.wait_ge(es_ready, 1 + it * PER + 2 * (B + 1))
                    nc.tensor.matmul(bank[7][:, 0:QB], ones[:], o_sq[:], start=True, stop=False)
                    for i in range(2):
                        mm = nc.tensor.matmul(bank[7][:, i * P:(i + 1) * P], es[(2 * B + i) % 4][:], ident[:],
                                              start=False, stop=i == 1)
                    mm.then_inc(ss_done, 1)

                with pe.Fori(0, 2) as it:
                    for L in range(-1, PER + 3):
                        items = plan.round(L)
                        for i, item in enumerate(items):
                            if item[0] == "s":
                                score(it, L + 1, *item[1:])
                            elif item[0] == "t":
                                turn(it, L - 1, *item[1:])
                            late = min(2, len(items) - 1)
                            if L % 2 == 1 and L >= 3 and i >= late:
                                values(it, L - 2, i - late, len(items) - late)
                            if L % 2 == 0 and L >= 4 and i == min(3, len(items) - 1):
                                square_sums(it, (L - 4) // 2)

            by_plan(pe, attend)

            pe.wait_ge(o_lo_done, 1 + VH * PAIR_BLOCKS)

            def merge(b, first=False):
                pe.wait_ge(br_loaded, (b + 1) * 64)
                for m in range(KT):
                    if first and m % 4 == 0:
                        pe.wait_ge(w3_lo_done, m + 4)
                    ms = slice(m * P, (m + 1) * P)
                    for br in range(2):
                        o = 2 * m + br
                        pe.wait_ge(y_gated, 1 + b * 2 * KT + max(o - 3, 0))
                        for k in range(4 * br, 4 * br + 4):
                            mm = split_product(bank[o % 4][:], (wa_hi[:, k, ms], wa_lo[:, k, ms]),
                                               (br_hi[:, k, :], br_lo[:, k, :]), k == 4 * br, k == 4 * br + 3)
                        mm.then_inc(y_done, 1)
                if first:
                    pe.wait_ge(w3_lo_done, 16)
                for i in range(QPB):
                    for half in range(2):
                        o = 2 * i + half
                        pe.wait_ge(f_out, 1 + b * 8 + max(o - 3, 0))
                        for k in range(KT):
                            if o == 0:
                                pe.wait_ge(m_lo_done, b * KT + (k + 1))
                            mm = split_product(bank[4 + o % 4][:], (m_hi[:, k, i * P:(i + 1) * P],
                                                                    m_lo[:, k, i * P:(i + 1) * P]),
                                               (wo_hi[:, k, half * 512:half * 512 + 512],
                                                wo_lo[:, k, half * 512:half * 512 + 512]), k == 0, k == KT - 1)
                        mm.then_inc(f_done, 1)

            merge(0, first=True)
            with pe.Fori(1, NB) as b:
                merge(b)

        @block.scalar
        def _(act):
            def split_w(dst, r):
                nc.scalar.activation(dst, raw[r % 2][:], ACT.Copy).then_inc(w_hi_done, 1)

            def norm_root(i):
                act.wait_ge(x_loaded[i % 2], 16 * (i // 2 + 1))
                if i >= 2:
                    act.wait_ge(x_turned, 2 * (i - 1))
                nc.scalar.activation(x_n[i % 2][:], x_in[i % 2][:], ACT.Square,
                                     accum_out=sums[:, 0, i:i + 1]).then_inc(x_squared, 1)
                act.wait_ge(x_squared, i + 1)
                nc.scalar.activation(sums[:, 1, i:i + 1], sums[:, 0, i:i + 1], ACT.Sqrt, bias=eps[:],
                                     scale=1.0 / D).then_inc(x_rooted, 1)

            def ht_split(i):
                for g in range(2):
                    act.wait_ge(x_turned, 2 * i + g + 1)
                    nc.scalar.activation(ht_hi[:, 4 * g:4 * g + 4, i * P:(i + 1) * P],
                                         bank[2 * (i % 2) + g][:].rearrange("p (k n) -> p k n", k=4), ACT.Copy
                                         ).then_inc(ht_hi_done, 1)

            act.wait_ge(consts_ready, 5)
            act.wait_ge(cols_in, 48)
            norm_root(0)
            norm_root(1)
            for r in range(4):
                act.wait_ge(raw_loaded[r % 2], 16 * (r // 2 + 1))
                split_w(wv_hi[:, 2 * r:2 * r + 2, :], r)
            ht_split(0)
            norm_root(2)
            ht_split(1)
            norm_root(3)
            for i in range(NT):
                if i + 2 < NT:
                    ht_split(i + 2)
                if i + 4 < NT:
                    norm_root(i + 4)
                act.wait_ge(v_done, i + 1)
                if i >= 4:
                    act.wait_ge(stored[i % 4], 16 * (i // 4))
                nc.scalar.activation(stage[i % 4][:, 0, :].bitcast(F32R), bank[4 + i % 4][:], ACT.Copy
                                     ).then_inc(v_hi_out, 1)

            def tile_w(n, par):
                act.wait_ge(raw_loaded[par], (n - par) * 8 + 48)
                nc.scalar.activation(w_hi[par][:], raw[par][:].rearrange("p (k c) -> p k c", k=KT), ACT.Copy
                                     ).then_inc(w_hi_done, 1)

            act.wait_ge(x_turned, 2 * NT)
            tile_w(0, 0)
            act.wait_ge(table_step, 14)
            nc.scalar.activation(cos_t[:], cos_t[:], ACT.Sin).then_inc(table_sin, 1)
            nc.scalar.activation(sin_t[:], sin_t[:], ACT.Sin, scale=rope_cols[:, 1:2]).then_inc(table_sin, 1)

            def project(n, j, it, kind, first):
                if not is_last(first, j, 1):
                    act.wait_ge(proj_done, 1 + n * NB)
                    tile_w(n + 1, (j + 1) % 2)
                for b in range(NB):
                    bk = bank[4 * (j % 2) + b]
                    if kind == "conv" and j < 3:
                        continue
                    if not (kind == "qk" and j == 0):
                        act.wait_ge(proj_done, 1 + n * NB + (b + 1))
                    if kind != "conv":
                        act.wait_ge(stored[b], stores_before(n, j, it, kind) * 16)
                    if kind == "gate":
                        nc.scalar.nop(nofuse=True)
                        nc.scalar.activation(stage[b][:, 0, :], bk[:], ACT.Sigmoid,
                                             bias=bias[:, bass.ds(n - G0, 1)]).then_inc(gate_done, 1)
                    elif kind == "z":
                        nc.scalar.activation(stage[b][:, 0, :], bk[:], ACT.Sigmoid).then_inc(sig_done, 1)
                    elif kind == "conv":
                        if b >= 2:
                            act.wait_ge(dve_done, done_before(n) + (b - 1))
                        else:
                            act.wait_ge(dve_done, done_before(n) - 4 * NB + 2 + b + 1 - 1)
                        nc.scalar.activation(tmp[b % 2][:], bk[:], ACT.Sigmoid).then_inc(sig_done, 1)
                        act.wait_ge(cv_done, it * NB + (b + 1))
                        nc.scalar.activation(stage[b][:, 0, :].bitcast(F32R), tmp[b % 2][:], ACT.Copy
                                             ).then_inc(hi_done, 1)
                    elif j == 0:
                        act.wait_ge(rot_sum, it * NB + (b + 1))
                        nc.scalar.activation(stage[b][:, 0, :].bitcast(F32R), tmp[0][:], ACT.Copy
                                             ).then_inc(hi_done, 1)
                    else:
                        nc.scalar.activation(stage[b][:, 0, :].bitcast(F32R), bk[:], ACT.Copy
                                             ).then_inc(hi_done, 1)

            sections(act, project)

            nc.scalar.preload_act_table_set("natural_log_exp_and_others")
            act.wait_ge(lam_step, 2)
            nc.scalar.activation(lam[:, 4:6], lam[:, 2:4], ACT.Exp).then_inc(lam_step, 1)

            def attend(plan):
                def exps(it, L):
                    act.wait_ge(nb_ready, it * PER + (L + 1))
                    for h, e in enumerate((e1[L % 3], e2[L % 2])):
                        e = e[:, 0:plan.keys(L)]
                        nc.scalar.activation(e, e, ACT.Exp, bias=nbias[L % 2][:, h:h + 1], scale=SCALE,
                                             accum_out=esum[L % 2][:, h:h + 1]).then_inc(exp_done, 1)

                def at_split(it, L, c, w):
                    if L % 2 == 0 and c == 0:
                        act.wait_ge(pv_done, 1 + it * (PER // 2) + max(L // 2 - 1, 0))
                    o = plan.before(L) + c // BLK
                    q0 = (L % 2) * P
                    act.wait_ge(turned, 1 + it * plan.CH + (o + 1))
                    nc.scalar.activation(at_hi[L // 2 % 2][:, c // P:(c + w) // P, q0:q0 + P],
                                         bank[4 + o % 2][:, 0:w].rearrange("p (k n) -> p k n", n=P), ACT.Copy
                                         ).then_inc(at_hi_done, 1)

                def square_o(it, B):
                    act.wait_ge(pv_done, 1 + it * (PER // 2) + (B + 1))
                    act.wait_ge(ss_done, 1 + it * (PER // 2) + B)
                    nc.scalar.activation(o_sq[:], bank[6][:, 0:QB], ACT.Square).then_inc(sq_done, 1)

                def inv_root(it, B):
                    act.wait_ge(ss_done, 1 + it * (PER // 2) + (B + 1))
                    act.wait_ge(o_normed, 1 + it * (PER // 2) + B)
                    nc.scalar.activation(o_r[:], bank[7][:, 0:QB], ACT.Ln, scale=1.0 / VD).then_inc(ln_done, 1)
                    act.wait_ge(ln_done, 1 + it * (PER // 2) + (B + 1))
                    nc.scalar.activation(o_r[:], o_r[:], ACT.Exp, scale=-0.5).then_inc(r_done, 1)

                def o_split(it, B):
                    act.wait_ge(o_gated, 1 + it * (PER // 2) + (B + 1))
                    act.wait_ge(att_stored[B % 2], 16 + it * 128 + 16 * (B // 2))
                    nc.scalar.activation(o_st[B % 2][:, 0, :].bitcast(F32R), o_n[:], ACT.Copy).then_inc(o_hi_done, 1)

                with act.Fori(0, 2) as it:
                    for L in range(-1, PER + 4):
                        if L % 2 == 1 and L >= 5:
                            o_split(it, (L - 5) // 2)
                        for item in plan.round(L):
                            if item[0] == "t":
                                at_split(it, L - 1, *item[1:])
                        if L % 2 == 1 and 3 <= L <= PER + 1:
                            square_o(it, (L - 3) // 2)
                        if L % 2 == 0 and L >= 4:
                            inv_root(it, (L - 4) // 2)
                        if L + 1 < PER:
                            exps(it, L + 1)

            by_plan(act, attend)

            def split_w3(i):
                act.wait_ge(w3_loaded[i], 16)
                if i < 8:
                    k0, cs = 2 * (i % 4), slice(i // 4 * 512, i // 4 * 512 + 512)
                    hi, r = wa_hi[:, k0:k0 + 2, cs], wa_raw[:, k0:k0 + 2, cs]
                else:
                    hi, r = wo_hi[:, i - 8, :], wo_raw[:, i - 8, :]
                nc.scalar.activation(hi, r, ACT.Copy).then_inc(w3_hi_done, 1)

            def merge(b, first=False):
                if not first:
                    act.wait_ge(f_done, 1 + b * 8)
                for m in range(KT):
                    act.wait_ge(m_sum, b * KT + (m + 1))
                    nc.scalar.activation(m_hi[:, m, :], ring[2 * m % 4][:], ACT.Copy).then_inc(m_hi_done, 1)
                    if first:
                        if m == 0:
                            for i in range(4, 8):
                                split_w3(i)
                        split_w3(8 + m)
                for i in range(QPB):
                    for half in range(2):
                        act.wait_ge(f_done, 1 + b * 8 + (2 * i + half + 1))
                        act.wait_ge(f_sq, 1 + b * 8 + (2 * i + half))
                        nc.scalar.activation(zeros[:], bank[4 + (2 * i + half) % 4][:], ACT.Square,
                                             accum_out=y_ss[i % 2][:, half:half + 1]).then_inc(f_sq, 1)
                    act.wait_ge(f_sum, b * QPB + (i + 1))
                    nc.scalar.activation(y_ss[i % 2][:, 3:4], y_ss[i % 2][:, 2:3], ACT.Sqrt, bias=eps[:],
                                         scale=1.0 / D).then_inc(f_root, 1)

            for i in range(4):
                split_w3(i)
            merge(0, first=True)
            with act.Fori(1, NB) as b:
                merge(b)

        @block.vector
        def _(dve):
            def split_w(dst, r):
                dve.wait_ge(w_hi_done, r + 1)
                nc.vector.tensor_tensor(dst[0], raw[r % 2][:].rearrange("p (k c) -> p k c", k=2),
                                        dst[1].bitcast(F32), ALU.subtract).then_inc(w_lo_done, 1)

            def norm(i):
                dve.wait_ge(x_rooted, i + 1)
                nc.vector.reciprocal(sums[:, 2, i:i + 1], sums[:, 1, i:i + 1]).then_inc(x_recip, 1)
                dve.wait_ge(x_recip, i + 1)
                if i >= 2:
                    dve.wait_ge(x_turned, 2 * (i - 1))
                nc.vector.scalar_tensor_tensor(out=x_n[i % 2][:], in0=x_in[i % 2][:], scalar=sums[:, 2, i:i + 1],
                                               in1=norm_w[:], op0=ALU.mult, op1=ALU.mult).then_inc(x_normed, 1)

            def ht_split(i):
                for g in range(2):
                    dve.wait_ge(ht_hi_done, 2 * i + g + 1)
                    cs = slice(i * P, (i + 1) * P)
                    nc.vector.tensor_tensor(ht_lo[:, 4 * g:4 * g + 4, cs],
                                            bank[2 * (i % 2) + g][:].rearrange("p (k n) -> p k n", k=4),
                                            ht_hi[:, 4 * g:4 * g + 4, cs].bitcast(F32), ALU.subtract
                                            ).then_inc(ht_lo_done, 1)

            dve.wait_ge(norm_in, 16)
            dve.wait_ge(consts_ready, 5)
            norm(0)
            norm(1)
            for r in range(4):
                split_w((wv_lo[:, 2 * r:2 * r + 2, :], wv_hi[:, 2 * r:2 * r + 2, :]), r)
            ht_split(0)
            norm(2)
            ht_split(1)
            norm(3)
            for i in range(NT):
                if i + 2 < NT:
                    ht_split(i + 2)
                if i + 4 < NT:
                    norm(i + 4)
                dve.wait_ge(v_hi_out, i + 1)
                nc.vector.tensor_tensor(stage[i % 4][:, 1, :].bitcast(F32R), bank[4 + i % 4][:],
                                        stage[i % 4][:, 0, :], ALU.subtract).then_inc(dve_done, 1)

            def tile_w(n, par):
                dve.wait_ge(w_hi_done, n + 5)
                nc.vector.tensor_tensor(w_lo[par][:], raw[par][:].rearrange("p (k c) -> p k c", k=KT),
                                        w_hi[par][:].bitcast(F32), ALU.subtract).then_inc(w_lo_done, 1)

            tile_w(0, 0)

            step = 0

            def linked(ins):
                nonlocal step
                step += 1
                ins.then_inc(table_step, 1)
                dve.wait_ge(table_step, step)

            def reduce_angle(out):
                for part in TURN:
                    linked(nc.vector.scalar_tensor_tensor(out=out, in0=cu[:, 0:S], scalar=-part, in1=out
                                                          if out is sin_ap else (sin_ap if part == TURN[0] else out),
                                                          op0=ALU.mult, op1=ALU.add))

            sin_ap, cos_ap = sin_t[:], cos_t[:]
            dve.wait_ge(pos_in, 16)
            dve.wait_ge(cols_in, 48)
            linked(nc.vector.tensor_scalar(sin_ap, cos_t[:].bitcast(I32), rope_cols[:, 0:1], None, ALU.mult))
            linked(nc.vector.tensor_scalar(cu[:, 0:S], sin_ap, 1 / (2 * np.pi), 0.25, ALU.mult, ALU.add))
            linked(nc.vector.tensor_scalar(cu[:, 0:S], cu[:, 0:S], ROUND, ROUND, ALU.add, ALU.subtract))
            reduce_angle(cos_ap)
            linked(nc.vector.tensor_scalar(cos_ap, cos_ap, np.pi / 2, PI_BELOW, ALU.add, ALU.min))
            linked(nc.vector.tensor_scalar(cos_ap, cos_ap, -PI_BELOW, None, ALU.max))
            linked(nc.vector.tensor_scalar(cu[:, 0:S], sin_ap, 1 / (2 * np.pi), ROUND, ALU.mult, ALU.add))
            linked(nc.vector.tensor_scalar(cu[:, 0:S], cu[:, 0:S], ROUND, None, ALU.subtract))
            reduce_angle(sin_ap)
            linked(nc.vector.tensor_scalar(sin_ap, sin_ap, PI_BELOW, -PI_BELOW, ALU.min, ALU.max))
            assert step == 14
            linked(nc.vector.memset(cu[:, 0:2], 0.0))

            def attend_first():
                dve.wait_ge(small_in, 16 * 5)
                for i in range(2):
                    nc.vector.tensor_tensor_reduce(lvec[:, 2 * i, :], lvec[:, 2 * i, :], lvec[:, 2 * i + 1, :], 1.0,
                                                   0.0, ALU.mult, ALU.add, lam[:, 2 + i:3 + i]).then_inc(lam_step, 1)
                nc.vector.tensor_scalar(sub_w[:, 1:2], sub_w[:, 0:1], 1.0 - LAMBDA_INIT, None, ALU.mult
                                        ).then_inc(flag_step, 1)
                nc.vector.memset(eps_fill[:], VD * SUB_EPS).then_inc(flag_step, 1)
                dve.wait_ge(chunk_in, 32)
                for c in (kc, qc):
                    nc.vector.tensor_scalar(c[:].bitcast(I32), c[:].bitcast(I32), CHUNK_SHIFT, None,
                                            ALU.arith_shift_right).then_inc(chunk_step, 1)
                dve.wait_ge(chunk_step, 2)
                for c in (kc, qc):
                    nc.vector.tensor_copy(c[:], c[:].bitcast(I32)).then_inc(chunk_step, 1)
                dve.wait_ge(chunk_step, 4)
                by_tile = kc[:].rearrange("p (t n) -> p t n", n=P)
                nc.vector.tensor_reduce(flags[:, 0, :], by_tile, AX_X, ALU.max).then_inc(flag_step, 1)
                nc.vector.tensor_reduce(flags[:, 1, :], by_tile, AX_X, ALU.min).then_inc(flag_step, 1)
                dve.wait_ge(flag_step, 4)
                nc.vector.tensor_tensor(flags[:, 2, 0:NT - 1], flags[:, 1, 1:NT], flags[:, 0, 0:NT - 1], ALU.is_gt
                                        ).then_inc(flag_step, 1)
                dve.wait_ge(flag_step, 5)
                nc.vector.tensor_reduce(flags[:, 3, 0:1], flags[:, 2, 0:NT - 1], AX_X, ALU.min).then_inc(flag_step, 1)
                dve.wait_ge(flag_step, 6)
                nc.vector.tensor_copy(causal_flag[:], flags[:, 3, 0:1]).then_inc(flag_ready, 1)

            def project(n, j, it, kind, first):
                if not is_last(first, j, 1):
                    tile_w(n + 1, (j + 1) % 2)
                if kind == "gate":
                    if first == G0 and j == 1:
                        attend_first()
                    return
                for b in range(NB):
                    bk = bank[4 * (j % 2) + b]
                    cs = slice(b * BLK, (b + 1) * BLK)
                    nth = it * NB + (b + 1)
                    hi, lo = stage[b][:, 0, :], stage[b][:, 1, :]
                    uses = stores_before(n, j, it, kind) * 16
                    if kind == "conv" or j == 0:
                        dve.wait_ge(dve_done, done_before(n) + b)
                    if kind == "z":
                        dve.wait_ge(sig_done, (n - Z0) * NB + (b + 1))
                        nc.vector.tensor_tensor(hi, bk[:], hi, ALU.mult).then_inc(dve_done, 1)
                    elif kind == "qk" and j > 0:
                        dve.wait_ge(hi_done, n * NB + (b + 1))
                        nc.vector.tensor_tensor(lo.bitcast(F32R), bk[:], hi, ALU.subtract).then_inc(dve_done, 1)
                    elif kind == "qk":
                        if b == 0:
                            dve.wait_ge(table_sin, 2)
                        dve.wait_ge(proj_done, 1 + n * NB + (b + 1))
                        nc.vector.tensor_tensor(tmp[0][:], bk[:], cos_t[:, cs], ALU.mult).then_inc(rot_cos, 1)
                        for a in (0, HD):
                            nc.vector.tensor_tensor(tmp[1][HD - a:P - a, :], bk[a:a + HD, :], sin_t[a:a + HD, cs],
                                                    ALU.mult).then_inc(rot_sin, 1)
                        dve.wait_ge(rot_cos, nth)
                        dve.wait_ge(rot_sin, it * (2 * NB) + 2 * (b + 1))
                        nc.vector.tensor_tensor(tmp[0][:], tmp[0][:], tmp[1][:], ALU.add).then_inc(rot_sum, 1)
                        dve.wait_ge(hi_done, n * NB + (b + 1))
                        nc.vector.tensor_tensor(lo.bitcast(F32R), tmp[0][:], hi, ALU.subtract).then_inc(dve_done, 1)
                    elif j == 0:
                        dve.wait_ge(proj_done, 1 + n * NB + (b + 1))
                        nc.vector.tensor_copy(cu[:, 2 + b * BLK:2 + (b + 1) * BLK], bk[:]).then_inc(dve_done, 1)
                    elif j == 1:
                        dve.wait_ge(proj_done, 1 + n * NB + (b + 1))
                        dve.wait_ge(dve_done, done_before(n) - NB + b + 1)
                        c = cu[:, 2 + b * BLK:2 + (b + 1) * BLK]
                        nc.vector.tensor_tensor(c, bk[:], c, ALU.mult).then_inc(dve_done, 1)
                    elif j == 2:
                        if b == 0:
                            dve.wait_ge(dve_done, done_before(n))
                        t0 = tmp[2][:]
                        x = [cu[:, b * BLK + d:(b + 1) * BLK + d] for d in range(3)]
                        w = [conv_w[:, bass.ds(it, 1), d:d + 1].rearrange("p o d -> p (o d)") for d in range(3)]
                        nc.vector.tensor_scalar(t0, x[0], w[0], None, ALU.mult).then_inc(tap0, 1)
                        dve.wait_ge(tap0, nth)
                        nc.vector.scalar_tensor_tensor(out=t0, in0=x[1], scalar=w[1], in1=t0, op0=ALU.mult,
                                                       op1=ALU.add).then_inc(tap1, 1)
                        dve.wait_ge(tap1, nth)
                        nc.vector.scalar_tensor_tensor(out=t0, in0=x[2], scalar=w[2], in1=t0, op0=ALU.mult,
                                                       op1=ALU.add).then_inc(tap2, 1)
                        dve.wait_ge(tap2, nth)
                        dve.wait_ge(proj_done, 1 + n * NB + (b + 1))
                        dve.wait_ge(stored[b], uses)
                        nc.vector.tensor_tensor(lo, bk[:], t0, ALU.mult).then_inc(dve_done, 1)
                    else:
                        t0 = tmp[b % 2][:]
                        dve.wait_ge(sig_done, Z_TILES * NB + nth)
                        nc.vector.tensor_tensor(t0, bk[:], t0, ALU.mult).then_inc(silu_done, 1)
                        dve.wait_ge(silu_done, nth)
                        dve.wait_ge(dve_done, done_before(n))
                        nc.vector.tensor_tensor(t0, t0, lo, ALU.mult).then_inc(cv_done, 1)
                        dve.wait_ge(hi_done, QK_TILES * NB + nth)
                        nc.vector.tensor_tensor(lo.bitcast(F32R), t0, hi, ALU.subtract).then_inc(dve_done, 1)

            sections(dve, project)

            dve.wait_ge(lam_step, 3)
            nc.vector.tensor_scalar(lam[:, 4:5], lam[:, 4:5], LAMBDA_INIT, None, ALU.add).then_inc(lam_step, 1)
            dve.wait_ge(lam_step, 4)
            nc.vector.tensor_tensor(lam[:, 0:1], lam[:, 5:6], lam[:, 4:5], ALU.subtract).then_inc(lam_step, 1)
            dve.wait_ge(lam_step, 5)

            def attend(plan):
                def mask_max(it, L, c, w, h):
                    if c == 0:
                        dve.wait_ge(turned, 1 + it * plan.CH + plan.before(max(L - 2, 0)))
                        dve.wait_ge(combined, 1 + it * PER + max(L - 1, 0))
                    masked = plan.masked(L, c)
                    if masked and h == 0:
                        m = plan.masks_before(L) + (0 if plan.causal else c // BLK)
                        dve.wait_ge(mask_ready, it * plan.MASKS + (m + 1))
                    o = 2 * (plan.before(L) + c // BLK) + h
                    dve.wait_ge(qk_done, it * 2 * plan.CH + (o + 1))
                    nc.vector.nop(nofuse=True)
                    m = plan.masks_before(L) + (0 if plan.causal else c // BLK)
                    e = e2[L % 2] if h else e1[L % 3]
                    nc.vector.tensor_tensor_reduce(e[:, c:c + w], bank[o % 4][:, 0:w],
                                                   mask[m % 2][:, 0:w] if masked else zeros[:, 0:w], 1.0, LOWEST,
                                                   ALU.add, ALU.max, mx[:, h, c // BLK:c // BLK + 1]
                                                   ).then_inc(scored, 1)

                def neg_max(it, L):
                    dve.wait_ge(scored, 1 + it * 2 * plan.CH + 2 * plan.before(L + 1))
                    nc.vector.tensor_reduce(m2[:], mx[:, :, 0:len(plan.chunks(L))], AX_X, ALU.max).then_inc(reduced, 1)
                    dve.wait_ge(reduced, it * PER + (L + 1))
                    nc.vector.tensor_scalar(nbias[L % 2][:], m2[:], -SCALE, None, ALU.mult).then_inc(nb_ready, 1)

                def combine(it, L):
                    s1, s2 = esum[L % 2][:, 0:1], esum[L % 2][:, 1:2]
                    dve.wait_ge(exp_done, it * 2 * PER + 2 * (L + 1))
                    nc.vector.reciprocal(ratio[:, 0:1], s2).then_inc(recip_done, 1)
                    dve.wait_ge(recip_done, it * PER + (L + 1))
                    nc.vector.scalar_tensor_tensor(out=ratio[:, 1:2], in0=ratio[:, 0:1], scalar=lam[:, 0:1], in1=s1,
                                                   op0=ALU.mult, op1=ALU.mult).then_inc(ratio_ready, 1)
                    dve.wait_ge(ratio_ready, it * PER + (L + 1))
                    a, b = e1[L % 3][:, 0:plan.keys(L)], e2[L % 2][:, 0:plan.keys(L)]
                    nc.vector.scalar_tensor_tensor(out=a, in0=b, scalar=ratio[:, 1:2], in1=a, op0=ALU.mult,
                                                   op1=ALU.add).then_inc(combined, 1)

                def scaled_eps(it, L):
                    s1 = esum[L % 2][:, 0:1]
                    dve.wait_ge(ss_done, 1 + it * (PER // 2) + max(L // 2 - 1, 0))
                    nc.vector.tensor_scalar(es[L % 4][:], eps_fill[:], s1, s1, ALU.mult, ALU.mult).then_inc(es_ready, 1)

                def at_split(it, L, c, w):
                    o = plan.before(L) + c // BLK
                    q0 = (L % 2) * P
                    dve.wait_ge(at_hi_done, it * plan.CH + (o + 1))
                    ks = slice(c // P, (c + w) // P)
                    nc.vector.tensor_tensor(at_lo[L // 2 % 2][:, ks, q0:q0 + P],
                                            bank[4 + o % 2][:, 0:w].rearrange("p (k n) -> p k n", n=P),
                                            at_hi[L // 2 % 2][:, ks, q0:q0 + P].bitcast(F32), ALU.subtract
                                            ).then_inc(at_lo_done, 1)

                def norm_o(it, B):
                    nth = it * (PER // 2) + (B + 1)
                    dve.wait_ge(o_lo_done, 1 + nth - 1)
                    dve.wait_ge(r_done, nth)
                    nc.vector.scalar_tensor_tensor(out=o_n[:], in0=bank[6][:, 0:QB], scalar=sub_w[:, 1:2], in1=o_r[:],
                                                   op0=ALU.mult, op1=ALU.mult).then_inc(o_normed, 1)
                    dve.wait_ge(o_normed, 1 + nth)
                    dve.wait_ge(z_loaded[B % 2], it * 128 + 16 * (B // 2 + 1))
                    nc.vector.tensor_tensor(o_n[:], o_n[:], z_in[B % 2][:], ALU.mult).then_inc(o_gated, 1)

                def o_split(it, B):
                    dve.wait_ge(o_hi_done, it * (PER // 2) + (B + 1))
                    nc.vector.tensor_tensor(o_st[B % 2][:, 1, :].bitcast(F32R), o_n[:], o_st[B % 2][:, 0, :],
                                            ALU.subtract).then_inc(o_lo_done, 1)

                with dve.Fori(0, 2) as it:
                    for L in range(-1, PER + 4):
                        items = plan.round(L)
                        for i, item in enumerate(items):
                            if item[0] == "s":
                                mask_max(it, L + 1, *item[1:])
                            elif item[0] == "t":
                                at_split(it, L - 1, *item[1:])
                            if i == min(0, len(items) - 1) and 0 <= L < PER:
                                combine(it, L)
                        if L + 1 < PER:
                            neg_max(it, L + 1)
                        if L % 2 == 1 and L >= 5:
                            o_split(it, (L - 5) // 2)
                        if 0 <= L < PER:
                            scaled_eps(it, L)
                        if L % 2 == 0 and L >= 4:
                            norm_o(it, (L - 4) // 2)

            by_plan(dve, attend)

            def split_w3(i):
                dve.wait_ge(w3_hi_done, i + 1)
                if i < 8:
                    k0, cs = 2 * (i % 4), slice(i // 4 * 512, i // 4 * 512 + 512)
                    hi, lo, r = wa_hi[:, k0:k0 + 2, cs], wa_lo[:, k0:k0 + 2, cs], wa_raw[:, k0:k0 + 2, cs]
                else:
                    hi, lo, r = wo_hi[:, i - 8, :], wo_lo[:, i - 8, :], wo_raw[:, i - 8, :]
                nc.vector.tensor_tensor(lo, r, hi.bitcast(F32), ALU.subtract).then_inc(w3_lo_done, 1)

            def merge(b, first=False):
                for m in range(KT):
                    for br in range(2):
                        o = 2 * m + br
                        dve.wait_ge(ring_loaded[o % 4], b * 96 + 16 * (o // 4 + 1))
                        dve.wait_ge(y_done, 1 + b * 2 * KT + (o + 1))
                        r = ring[o % 4][:]
                        nc.vector.tensor_tensor(r, bank[o % 4][:], r, ALU.mult).then_inc(y_gated, 1)
                    dve.wait_ge(y_gated, 1 + b * 2 * KT + 2 * (m + 1))
                    ra, rc = ring[2 * m % 4][:], ring[(2 * m + 1) % 4][:]
                    nc.vector.tensor_tensor(ra, ra, rc, ALU.add).then_inc(m_sum, 1)
                    dve.wait_ge(m_hi_done, b * KT + (m + 1))
                    nc.vector.tensor_tensor(m_lo[:, m, :], ra, m_hi[:, m, :].bitcast(F32), ALU.subtract
                                            ).then_inc(m_lo_done, 1)
                    if first:
                        if m == 0:
                            for i in range(4, 8):
                                split_w3(i)
                        split_w3(8 + m)
                for i in range(QPB):
                    ss = y_ss[i % 2]
                    dve.wait_ge(f_sq, 1 + b * 8 + 2 * (i + 1))
                    nc.vector.tensor_tensor(ss[:, 2:3], ss[:, 0:1], ss[:, 1:2], ALU.add).then_inc(f_sum, 1)
                    dve.wait_ge(f_root, b * QPB + (i + 1))
                    nc.vector.reciprocal(ss[:, 2:3], ss[:, 3:4]).then_inc(f_recip, 1)
                    dve.wait_ge(f_recip, b * QPB + (i + 1))
                    for half in range(2):
                        o = 2 * i + half
                        bk = bank[4 + o % 4][:]
                        nc.vector.scalar_tensor_tensor(out=bk, in0=bk, scalar=ss[:, 2:3],
                                                       in1=post_w[:, half * 512:half * 512 + 512], op0=ALU.mult,
                                                       op1=ALU.mult).then_inc(f_scaled, 1)
                    for half in range(2):
                        o = 2 * i + half
                        dve.wait_ge(f_scaled, b * 8 + (o + 1))
                        dve.wait_ge(ring_loaded[o % 4], b * 96 + 16 * ((16 + o) // 4 + 1))
                        nc.vector.tensor_tensor(ring[o % 4][:], bank[4 + o % 4][:], ring[o % 4][:], ALU.add
                                                ).then_inc(f_out, 1)

            for i in range(4):
                split_w3(i)
            dve.wait_ge(post_in, 16)
            merge(0, first=True)
            with dve.Fori(1, NB) as b:
                merge(b)


def feature_order():
    head = np.arange(SH)[:, None] * HD
    one = np.concatenate([(head + np.arange(HALF)).ravel(), (head + HALF + np.arange(HALF)).ravel(),
                          (head + ROPE + np.arange(REST)).ravel()])
    q0, k0, z0, b0, c0, u0, zc0, g0 = 0, 512, 1536, 2048, 2560, 3072, 3584, 4096
    order = [q0 + one, k0 + one, z0 + np.arange(WIDTH)]
    for c in range(4):
        order += [o + c * P + np.arange(P) for o in (c0, u0, b0, zc0)]
    return np.concatenate(order + [g0 + np.arange(2 * D)])


V0 = 2 * WIDTH


def kernel(**inputs):
    import concourse.bacc as bacc
    from concourse.bass_utils import run_bass_kernel_spmd

    a = {k: np.asarray(v) for k, v in inputs.items()}
    w = a["w_in"][0]
    tiles = w[:, feature_order()].reshape(KT, P, N_TILES, P).transpose(2, 1, 0, 3)
    v = w[:, V0:V0 + WIDTH].reshape(4, 2, P, WIDTH).transpose(0, 2, 1, 3)
    freq = (THETA ** (-np.arange(0, ROPE, 2, dtype=np.float64) / ROPE)).astype(np.float32)
    rope = np.stack([np.tile(freq, 2 * SH), np.repeat(np.float32([1, -1]), HD)], axis=1)
    arrays = {
        "x": a["x"][0], "positions": a["positions"].reshape(1, S), "pre_norm_w": a["pre_norm_w"].reshape(1, D),
        "w_in": tiles.reshape(N_TILES * P, D), "w_v": v.reshape(4, P, 2 * WIDTH),
        "rope_cols": rope, "bias": a["merge_bias"][0].reshape(GATE_TILES, P).T,
        "conv_w": a["conv_w"][0, :, 0].reshape(3, 4, P).transpose(2, 1, 0),
        "subln_w": a["subln_w"].reshape(VD, 1),
        "positions_by_tile": a["positions"].reshape(NT, P).T, "w_att_out": a["w_att_out"][0], "w_conv_out": a["w_conv_out"][0],
        "w_out": a["w_out"][0], "post_norm_w": a["post_norm_w"].reshape(1, D),
    }
    for name in ("lambda_q1", "lambda_k1", "lambda_q2", "lambda_k2"):
        arrays[name] = a[name].reshape(1, HD)
    nc = bacc.Bacc("TRN2", target_bir_lowering=False, num_devices=1)
    feed, tensors = {}, {}
    for name, value in arrays.items():
        value = np.ascontiguousarray(value)
        feed[f"in_{name}"] = value
        tensors[name] = nc.dram_tensor(f"in_{name}", value.shape, mybir.dt.from_np(value.dtype),
                                       kind="ExternalInput").ap()
    tensors["out"] = nc.dram_tensor("out_0", (S, D), F32, kind="ExternalOutput").ap()
    build(nc, tensors)
    r = run_bass_kernel_spmd(nc, [feed], core_ids=[0])
    return r.results[0]["out_0"].reshape(1, S, D)
```
